# Optimizing a Trainium2 kernel written in Bass

```python
import math
import jax
import jax.numpy as jnp
from jax import lax
import numpy as np

D_MODEL = 1024
BATCH = 1
SEQ = 256
DEPTH = 1

HEAD_DIM = 64
N_MOBA_HEADS = 4
MOBA_BLOCK = 256
MOBA_TOPK = 3
MOBA_Q_CHUNK = 32
N_DIFF_HEADS = 4
DIFF_HEAD_DIM = 32
DIFF_Q_BLOCK = 128
N_POOL_GROUPS = 4
POOL_GROUP = 64
POOL_WINDOWS = (2, 4, 8, 16)
N_DSA_HEADS = 4
N_IDX_HEADS = 4
IDX_HEAD_DIM = 32
DSA_TOPK = 256
DSA_Q_CHUNK = 64
N_BRANCHES = 4
BRANCH_WIDTH = 256
D_FF = 4 * D_MODEL
N_ALIBI_HEADS = N_MOBA_HEADS + N_DIFF_HEADS + N_DSA_HEADS
NORM_EPS = 1e-6
NEG_INF = -1e30

MOBA_W = N_MOBA_HEADS * HEAD_DIM
DIFF_W = N_DIFF_HEADS * 2 * DIFF_HEAD_DIM
POOL_W = N_POOL_GROUPS * POOL_GROUP
DSA_W = N_DSA_HEADS * HEAD_DIM
IDX_Q_W = N_IDX_HEADS * IDX_HEAD_DIM
IN_SPLITS = (MOBA_W, MOBA_W, MOBA_W, DIFF_W, DIFF_W, DIFF_W, POOL_W,
             DSA_W, DSA_W, DSA_W, IDX_Q_W, IDX_HEAD_DIM, N_IDX_HEADS)
IN_PROJ_WIDTH = 3 * MOBA_W + 3 * DIFF_W + POOL_W + 3 * DSA_W + IDX_Q_W + IDX_HEAD_DIM + N_IDX_HEADS

kernel_name = 'hybrid_gated_moba_diff_pool_dsa'

def rms_norm(x, g):
    xf = x.astype(jnp.float32)
    y = xf * lax.rsqrt(jnp.mean(xf * xf, axis=-1, keepdims=True) + NORM_EPS)
    return (y * g.astype(jnp.float32)).astype(x.dtype)

def alibi_slopes():
    n = N_ALIBI_HEADS
    return jnp.asarray(2.0 ** (-8.0 * np.arange(1, n + 1) / n), dtype=jnp.float32)

def _chunks(fn, seq, size):
    starts = jnp.arange(seq // size, dtype=jnp.int32) * size
    out = jnp.moveaxis(lax.map(fn, starts), 0, 1)
    return out.reshape((out.shape[0], seq) + out.shape[3:])

def moba_attention(q, k, v, slopes):
    B, S, H, Dh = q.shape
    f32 = jnp.float32
    q, k, v = q.astype(f32), k.astype(f32), v.astype(f32)
    n_blk = -(-S // MOBA_BLOCK)
    pad = ((0, 0), (0, n_blk * MOBA_BLOCK - S), (0, 0), (0, 0))
    kp, vp = jnp.pad(k, pad), jnp.pad(v, pad)
    kb = kp.reshape(B, n_blk, MOBA_BLOCK, H, Dh).transpose(0, 3, 1, 2, 4)
    vb = vp.reshape(B, n_blk, MOBA_BLOCK, H, Dh).transpose(0, 3, 1, 2, 4)
    k_mean = kb.mean(axis=3)
    n_sel = min(MOBA_TOPK, n_blk)
    scale = Dh ** -0.5
    blk_ids = jnp.arange(n_blk)
    offs = jnp.arange(MOBA_BLOCK)
    b_ix = jnp.arange(B)[:, None, None, None]
    h_ix = jnp.arange(H)[None, None, :, None]
    m = slopes[None, None, :, None]

    def chunk(start):
        qc = lax.dynamic_slice_in_dim(q, start, MOBA_Q_CHUNK, axis=1)
        t = start + jnp.arange(MOBA_Q_CHUNK)
        cur = start // MOBA_BLOCK
        gate = jnp.einsum('bqhd,bhnd->bqhn', qc, k_mean)
        gate = jnp.where(blk_ids < cur, gate, NEG_INF)
        _, sel = lax.top_k(gate, n_sel)
        kg = kb[b_ix, h_ix, sel]
        vg = vb[b_ix, h_ix, sel]
        s_sel = jnp.einsum('bqhd,bqhnkd->bqhnk', qc, kg) * scale
        pos_sel = sel[..., None] * MOBA_BLOCK + offs
        dist_sel = (t[None, :, None, None, None] - pos_sel).astype(f32)
        s_sel = jnp.where((sel < cur)[..., None], s_sel - m[..., None] * dist_sel, NEG_INF)
        k_own = lax.dynamic_slice_in_dim(kp, cur * MOBA_BLOCK, MOBA_BLOCK, axis=1)
        v_own = lax.dynamic_slice_in_dim(vp, cur * MOBA_BLOCK, MOBA_BLOCK, axis=1)
        s_own = jnp.einsum('bqhd,bkhd->bqhk', qc, k_own) * scale
        dist_own = (t[:, None] - (cur * MOBA_BLOCK + offs)[None, :]).astype(f32)[None, :, None, :]
        s_own = jnp.where(dist_own >= 0, s_own - m * dist_own, NEG_INF)
        s_all = jnp.concatenate([s_sel.reshape(B, MOBA_Q_CHUNK, H, n_sel * MOBA_BLOCK), s_own], axis=-1)
        p = jax.nn.softmax(s_all, axis=-1)
        p_sel = p[..., :n_sel * MOBA_BLOCK].reshape(B, MOBA_Q_CHUNK, H, n_sel, MOBA_BLOCK)
        p_own = p[..., n_sel * MOBA_BLOCK:]
        return (jnp.einsum('bqhnk,bqhnkd->bqhd', p_sel, vg)
                + jnp.einsum('bqhk,bkhd->bqhd', p_own, v_own))

    return _chunks(chunk, S, MOBA_Q_CHUNK)

def diff_attention(q, k, v, slopes, lam, lambda_init, subln_g):
    B, S, H, _, dh = q.shape
    f32 = jnp.float32
    q, k, v = q.astype(f32), k.astype(f32), v.astype(f32)
    scale = dh ** -0.5
    s_pos = jnp.arange(S)
    m = slopes[:, None, None, None]

    def block(start):
        qb = lax.dynamic_slice_in_dim(q, start, DIFF_Q_BLOCK, axis=1)
        t = start + jnp.arange(DIFF_Q_BLOCK)
        dist = (t[:, None] - s_pos[None, :]).astype(f32)
        s = jnp.einsum('bqhmd,bshmd->bhmqs', qb, k) * scale
        s = jnp.where(dist >= 0, s - m * dist, NEG_INF)
        p = jax.nn.softmax(s, axis=-1)
        a = p[:, :, 0] - lam * p[:, :, 1]
        return jnp.einsum('bhqs,bshe->bqhe', a, v)

    o = _chunks(block, S, DIFF_Q_BLOCK)
    o = o * lax.rsqrt(jnp.mean(o * o, axis=-1, keepdims=True) + NORM_EPS) * subln_g
    return o * (1.0 - lambda_init)

def pool_mixer(u, w_pool, pool_scale):
    B, S, _ = u.shape
    uf = u.astype(jnp.float32)
    cs = jnp.cumsum(uf, axis=1)
    t = jnp.arange(S)
    outs = []
    for g, w in enumerate(POOL_WINDOWS):
        c_g = cs[..., g * POOL_GROUP:(g + 1) * POOL_GROUP]
        lower = jnp.pad(c_g[:, :S - w], ((0, 0), (w, 0), (0, 0)))
        cnt = jnp.minimum(t + 1, w).astype(jnp.float32)[None, :, None]
        outs.append((c_g - lower) / cnt - uf[..., g * POOL_GROUP:(g + 1) * POOL_GROUP])
    d = jnp.stack(outs, axis=2)
    y = jnp.einsum('bsgc,gce->bsge', d, w_pool).reshape(B, S, POOL_W)
    return (y * pool_scale).astype(u.dtype)

def dsa_attention(q, k, v, iq, ik, iw, slopes):
    B, S, H, Dh = q.shape
    f32 = jnp.float32
    q, k, v = q.astype(f32), k.astype(f32), v.astype(f32)
    iq, ik = iq.astype(f32), ik.astype(f32)
    iw = iw.astype(f32) * N_IDX_HEADS ** -0.5
    n_sel = min(DSA_TOPK, S // 4)
    s_pos = jnp.arange(S)
    b_ix = jnp.arange(B)[:, None, None]
    m = slopes[None, None, :, None]

    def chunk(start):
        qc = lax.dynamic_slice_in_dim(q, start, DSA_Q_CHUNK, axis=1)
        iqc = lax.dynamic_slice_in_dim(iq, start, DSA_Q_CHUNK, axis=1)
        iwc = lax.dynamic_slice_in_dim(iw, start, DSA_Q_CHUNK, axis=1)
        t = start + jnp.arange(DSA_Q_CHUNK)
        rel = jax.nn.relu(jnp.einsum('bqhd,bsd->bqhs', iqc, ik) * IDX_HEAD_DIM ** -0.5)
        score = jnp.einsum('bqhs,bqh->bqs', rel, iwc)
        score = jnp.where(s_pos[None, None, :] <= t[None, :, None], score, NEG_INF)
        _, sel = lax.top_k(score, n_sel)
        kg = k[b_ix, sel]
        vg = v[b_ix, sel]
        dist = (t[None, :, None] - sel).astype(f32)[:, :, None, :]
        s = jnp.einsum('bqhd,bqnhd->bqhn', qc, kg) * Dh ** -0.5
        s = jnp.where(dist >= 0, s - m * dist, NEG_INF)
        p = jax.nn.softmax(s, axis=-1)
        return jnp.einsum('bqhn,bqnhd->bqhd', p, vg)

    return _chunks(chunk, S, DSA_Q_CHUNK)

def hybrid_layer(x, c_act, layer, slopes, w_ada, b_ada, norm1_g, w_in, diff_lambda, diff_subln_g,
                 w_pool, pool_scale, w_gate, b_gate, w_branch, w_out, norm2_g, w_ff1, w_ff2):
    B, S, D = x.shape
    f32 = jnp.float32
    mod = (c_act @ w_ada + b_ada)[:, None, :]
    sh1, sc1, g1, sh2, sc2, g2 = jnp.split(mod, 6, axis=-1)
    h = rms_norm(x, norm1_g) * (1.0 + sc1) + sh1
    proj = h @ w_in
    offsets = np.cumsum(IN_SPLITS)[:-1].tolist()
    aq, ak, av, bq, bk, bv, pu, dq, dk, dv, iq, ik, iw = jnp.split(proj, offsets, axis=-1)
    slopes_a, slopes_b, slopes_d = slopes[0::3], slopes[1::3], slopes[2::3]

    y_a = moba_attention(aq.reshape(B, S, N_MOBA_HEADS, HEAD_DIM), ak.reshape(B, S, N_MOBA_HEADS, HEAD_DIM),
                         av.reshape(B, S, N_MOBA_HEADS, HEAD_DIM), slopes_a).reshape(B, S, MOBA_W)

    lambda_init = 0.8 - 0.6 * math.exp(-0.3 * layer)
    lq1, lk1, lq2, lk2 = diff_lambda.astype(f32)
    lam = jnp.exp(jnp.sum(lq1 * lk1)) - jnp.exp(jnp.sum(lq2 * lk2)) + lambda_init
    qk_shape = (B, S, N_DIFF_HEADS, 2, DIFF_HEAD_DIM)
    y_b = diff_attention(bq.reshape(qk_shape), bk.reshape(qk_shape),
                         bv.reshape(B, S, N_DIFF_HEADS, 2 * DIFF_HEAD_DIM), slopes_b, lam, lambda_init,
                         diff_subln_g.astype(f32)).reshape(B, S, DIFF_W)

    y_c = pool_mixer(pu, w_pool, pool_scale)

    y_d = dsa_attention(dq.reshape(B, S, N_DSA_HEADS, HEAD_DIM), dk.reshape(B, S, N_DSA_HEADS, HEAD_DIM),
                        dv.reshape(B, S, N_DSA_HEADS, HEAD_DIM), iq.reshape(B, S, N_IDX_HEADS, IDX_HEAD_DIM),
                        ik, iw, slopes_d).reshape(B, S, DSA_W)

    terms = []
    for i, y in enumerate((y_a, y_b, y_c, y_d)):
        gate = jax.nn.sigmoid((h @ w_gate[i] + b_gate[i]).astype(f32))
        terms.append(gate * (y.astype(x.dtype) @ w_branch[i]))
    merged = (terms[0] + terms[1] + terms[2] + terms[3]).astype(x.dtype)
    x = x + g1 * (merged @ w_out)

    h2 = rms_norm(x, norm2_g) * (1.0 + sc2) + sh2
    ff = jnp.square(jax.nn.relu(h2 @ w_ff1)) @ w_ff2
    return x + g2 * ff

def setup_inputs(seed: int = 0) -> dict:
    key = jax.random.key(seed)
    ks = jax.random.split(key, 20)
    D = D_MODEL

    def nrm(k, shape, scale):
        return jax.random.normal(k, shape, jnp.float32) * scale

    return {
        'x': nrm(ks[0], (BATCH, SEQ, D), 1.0),
        'c': nrm(ks[1], (BATCH, D), 1.0),
        'w_ada': nrm(ks[2], (DEPTH, D, 6 * D), 0.5 * D ** -0.5),
        'b_ada': nrm(ks[3], (DEPTH, 6 * D), 0.02),
        'norm1_g': 1.0 + nrm(ks[4], (DEPTH, D), 0.02),
        'w_in': nrm(ks[5], (DEPTH, D, IN_PROJ_WIDTH), D ** -0.5),
        'diff_lambda': nrm(ks[6], (DEPTH, 4, DIFF_HEAD_DIM), 0.1),
        'diff_subln_g': 1.0 + nrm(ks[7], (DEPTH, 2 * DIFF_HEAD_DIM), 0.02),
        'w_pool': nrm(ks[8], (DEPTH, N_POOL_GROUPS, POOL_GROUP, POOL_GROUP), POOL_GROUP ** -0.5),
        'pool_scale': 1.0 + nrm(ks[9], (DEPTH, POOL_W), 0.1),
        'w_gate': nrm(ks[10], (DEPTH, N_BRANCHES, D, D), D ** -0.5),
        'b_gate': nrm(ks[11], (DEPTH, N_BRANCHES, D), 0.02),
        'w_branch': nrm(ks[12], (DEPTH, N_BRANCHES, BRANCH_WIDTH, D), BRANCH_WIDTH ** -0.5),
        'w_out': nrm(ks[13], (DEPTH, D, D), D ** -0.5),
        'norm2_g': 1.0 + nrm(ks[14], (DEPTH, D), 0.02),
        'w_ff1': nrm(ks[15], (DEPTH, D, D_FF), D ** -0.5),
        'w_ff2': nrm(ks[16], (DEPTH, D_FF, D), D_FF ** -0.5),
        'final_norm_g': 1.0 + nrm(ks[17], (D,), 0.02),
    }

def reference(x, c, w_ada, b_ada, norm1_g, w_in, diff_lambda, diff_subln_g, w_pool, pool_scale,
              w_gate, b_gate, w_branch, w_out, norm2_g, w_ff1, w_ff2, final_norm_g):
    slopes = alibi_slopes()
    c_act = jax.nn.silu(c)
    for l in range(DEPTH):
        x = hybrid_layer(x, c_act, l, slopes, w_ada[l], b_ada[l], norm1_g[l], w_in[l], diff_lambda[l],
                         diff_subln_g[l], w_pool[l], pool_scale[l], w_gate[l], b_gate[l], w_branch[l],
                         w_out[l], norm2_g[l], w_ff1[l], w_ff2[l])
    return rms_norm(x, final_norm_g)


_drawn_inputs = setup_inputs


def setup_inputs(seed=0):
    import zlib

    import numpy as np

    out = dict(_drawn_inputs(seed))
    spreads = {}
    factors = {'norm1_g': 4.557,
     'diff_lambda': 8.0,
     'diff_subln_g': 53.653,
     'pool_scale': 3.74,
     'b_gate': 8.0,
     'norm2_g': 19.935,
     'final_norm_g': 24.362}
    for name, (base, spread) in spreads.items():
        noise = np.random.default_rng([zlib.crc32(name.encode()), seed]).standard_normal(out[name].shape)
        drawn = base * np.exp(spread * noise) if base else spread * noise
        out[name] = jnp.asarray(drawn.astype(out[name].dtype))
    for name, factor in factors.items():
        out[name] = (out[name] * factor).astype(out[name].dtype)
    return out
```

```python
import math
from contextlib import ExitStack

import numpy as np
import concourse.bass as bass
from concourse import mybir

P = 128
SEQ = 256
DM = 1024
KT = DM // P
TT = SEQ // P
SC = 256
SLAB = KT * SC
NP = DM // SC
DFF = 4 * DM
NH = 4
HD = 64
DHD = 32
IDXW = NH * DHD + DHD + NH
TOPK = SEQ // 4
EPS = 1e-6
NEG = -1e30
TAKEN = -3e38
LAMBDA_INIT = 0.8 - 0.6 * math.exp(-0.3 * 0)
WINDOWS = (2, 4, 8, 16)
PAD = 16
N_SLOPES = 3 * NH
RAW = 3
SPL = 4
LEAD = 3

F32 = mybir.dt.float32
F32R = mybir.dt.float32r
BF16 = mybir.dt.bfloat16
I32 = mybir.dt.int32
ALU = mybir.AluOpType
ACT = mybir.ActivationFunctionType
AX = mybir.AxisListType.X

COL = {}
_at = 0
for _name in ("aq", "ak", "av", "bq", "bk", "bv", "pu", "dq", "dk", "dv"):
    COL[_name] = _at
    _at += SC
COL["idx"] = _at

PROJ = ["idx", "dq", "dk", "aq", "ak", "av", "bq", "bk", "bv", "pu", "dv"]
MIXERS = ["a", "c", "b", "d"]
W = [("proj", n, 0) for n in PROJ]
for _m in MIXERS:
    W += [("gate", _m, n) for n in range(NP)] + [("branch", _m, 0)]
W += [("out", "", n) for n in range(NP)]
NW = len(W)
J = {w: j for j, w in enumerate(W)}
JP = {n: J[("proj", n, 0)] for n in PROJ}

GRING = 3
G = []
_g = 0
for _w in W:
    G.append(_g)
    _g += NP if _w[0] == "branch" else 1
EMPTY = {}
USES = [0] * GRING
for _w, _g in zip(W, G):
    if _w[0] == "branch":
        for _n in range(NP):
            EMPTY[_g + _n] = ("prod", NP * MIXERS.index(_w[1]) + _n + 1)
    elif _w[0] == "out":
        EMPTY[_g] = ("x2", _w[2] + 1)
    else:
        USES[_g % GRING] += 1
        EMPTY[_g] = ("bank", USES[_g % GRING])

ADA = list(range(4, 24))
ADA0 = 4
ADA_GROUP = {j: ADA0 + i for i, j in enumerate((6, 9, 12, 14, 17, 18, 21, 22, 23, 26, 27, 28))}
ORDER = [("ada", 0), ("ada", 1), ("w", 0), ("ada", 2), ("ada", 3)] + [("w", j) for j in range(1, LEAD)]
for _j in range(NW):
    if _j + LEAD < NW:
        ORDER.append(("w", _j + LEAD))
    if _j in ADA_GROUP:
        ORDER.append(("ada", ADA_GROUP[_j]))
POS = {x: s for s, x in enumerate(ORDER)}
NORD = len(ORDER)
FADA = ADA0 + len(ADA_GROUP)
FF_SLABS = 2 * NP
FF_ALL = FF_SLABS + 1
assert FF_ALL % RAW == 0 and FF_SLABS % SPL == 0

VROW = {"c": 0, "b_ada": 8, "norm1": 56, "norm2": 64, "b_gate": 72, "pool": 104}
NVEC = 106


def slope(h):
    return 2.0 ** (-8.0 * (h + 1) / N_SLOPES)


class Count:

    def __init__(self, sem):
        self.sem, self.n = sem, 0

    def inc(self, instruction):
        self.n += 1
        instruction.then_inc(self.sem, 1)
        return self.n


def build(nc, x, c, w_ada, b_ada, norm1_g, w_in, diff_lambda, diff_subln_g, w_pool, pool_scale,
          w_gate, b_gate, w_branch, w_out, norm2_g, w_ff1, w_ff2, final_norm_g, out):
    with ExitStack() as ctx:
        def sb(name, shape, dt=F32):
            return ctx.enter_context(nc.sbuf_tensor(name, shape, dt))

        def over(name, at, shape):
            return nc.alloc_sbuf_tensor_at(name, shape, F32R, offset=at)

        def sem(name):
            return ctx.enter_context(nc.semaphore(name))

        raw = sb("raw", [P, RAW, SLAB])
        w_hi = sb("w_hi", [P, SPL, SLAB], F32R)
        w_lo = sb("w_lo", [P, SPL, SLAB], F32R)
        h_hi = sb("h_hi", [P, KT, SEQ], F32R)
        h_lo = sb("h_lo", [P, KT, SEQ], F32R)
        iw_hi = sb("iw_hi", [P, KT, NH], F32R)
        iw_lo = sb("iw_lo", [P, KT, NH], F32R)
        xT = sb("xT", [P, KT, SEQ])
        mix_at = nc.sbuf_base
        mix = sb("mix", [P, 16 * SEQ + 2 * (PAD + SEQ)])
        def part(at, n):
            return mix[:, at * SEQ:(at + n) * SEQ].rearrange("p (t s) -> p t s", s=SEQ)
        qk_a, qk_b = part(0, 2), part(2, 2)
        dqT, dkT = part(4, 2), part(6, 2)
        v0, v1 = part(8, 2), part(10, 2)
        idxT = part(12, 2)
        uT = mix[:, 14 * SEQ:14 * SEQ + 2 * (PAD + SEQ)].rearrange("p (t s) -> p t s", s=PAD + SEQ)
        f_hi = over("f_hi", mix_at, [P, KT, SEQ])
        f_lo = over("f_lo", mix_at + 4 * KT * SEQ, [P, KT, SEQ])
        NB = NH * (P + SEQ)
        big_at = nc.sbuf_base
        big = sb("big", [P, 3 * NB])
        bias = [big[:, i * NB:(i + 1) * NB] for i in range(3)]
        g_hi = over("g_hi", big_at, [P, KT, SEQ])
        g_lo = over("g_lo", big_at + 4 * KT * SEQ, [P, KT, SEQ])
        gf = big[:, 0:DM]
        scratch = sb("scratch", [P, 2 * NB])
        prob, probT = scratch[:, 0:NB], scratch[:, NB:2 * NB]
        sq = scratch[:, 0:KT * SEQ].rearrange("p (t s) -> p t s", s=SEQ)
        score = sb("score", [P, P + SEQ])
        causal = sb("causal", [P, P + SEQ])
        y_hi = sb("y_hi", [P, 2, 2, SEQ], F32R)
        y_lo = sb("y_lo", [P, 2, 2, SEQ], F32R)
        yn = sb("yn", [P, 2 * SEQ])
        tg = sb("tg", [P, NP, 2 * SEQ])
        x_nat = tg[:, :, :].rearrange("p a b -> p (a b)").rearrange("p (t d) -> p t d", t=TT)
        prod = sb("prod", [P, 2, 2 * SEQ])
        merged = sb("merged", [P, KT * SEQ])
        xn = merged[:, :].rearrange("p (t s) -> p t s", s=SEQ)
        acc = sb("acc", [P, 2, 2, SC])
        win = sb("win", [P, 2, PAD + SEQ])
        icnt = sb("icnt", [P, 2, SEQ])
        shift_w = ([mix[:, i * SLAB:(i + 1) * SLAB].rearrange("p (k n) -> p k n", k=KT) for i in range(2)]
                   + [big[:, i * SLAB:(i + 1) * SLAB].rearrange("p (k n) -> p k n", k=KT) for i in range(2)])
        shift_rows = [prod[0:1, i, :] for i in range(2)]
        iwT = prod[0:NH, 0, 0:SEQ]
        rstd = sb("rstd", [P, SEQ])
        root = sb("root", [P, 4])
        ones = sb("ones", [P, P])
        ident = sb("ident", [P, P])
        zeros = sb("zeros", [P, P], BF16)
        wpool = sb("wpool", [P, 2, P])
        vec = sb("vec", [P, P])
        vT = sb("vT", [P, NVEC])
        mod = sb("mod", [P, 48])
        aff = sb("aff", [P, 2, KT])
        cact = sb("cact", [P, 2, KT])
        hgate = sb("hgate", [P, NH * KT])
        lamw = sb("lamw", [P, 4 * DHD])
        lams = sb("lams", [P, 8])
        subg = sb("subg", [P, HD])
        eps = sb("eps", [P, 1])
        top8 = sb("top8", [P, 2, 8])
        iw = sb("iw", [P, TT, NH])
        smax = sb("smax", [P, 8])
        nmax = sb("nmax", [P, 8])
        rsum = sb("rsum", [P, 8])
        rinv = sb("rinv", [P, 8])
        rs = sb("rs", [P, 4, 8])

        bank = [ctx.enter_context(nc.psum_tensor(f"bank{b}", [P, 512], F32)) for b in range(3)]
        att = ctx.enter_context(nc.psum_tensor("att", [P, 3, 512], F32))
        adab = ctx.enter_context(nc.psum_tensor("adab", [P, 512], F32))
        misc = ctx.enter_context(nc.psum_tensor("misc", [P, 512], F32))
        attf = att[:, :, :].rearrange("p b n -> p (b n)")
        accb = [att[:, 0, :], att[:, 1, :], att[:, 2, :], misc[:, :]]
        natb = [bank[0][:, :], bank[1][:, :], bank[2][:, :], adab[:, :]]

        raw_landed = [sem(f"raw_landed{i}") for i in range(RAW)]
        x_landed = sem("x_landed")
        shift_landed = [sem(f"shift_landed{i}") for i in range(NP)]
        cact_ready = sem("cact_ready")
        row_ready = sem("row_ready")
        row_read = sem("row_read")
        diag_ready = sem("diag_ready")
        wide_ready = sem("wide_ready")
        vec_landed = sem("vec_landed")
        small_landed = sem("small_landed")
        gf_landed = sem("gf_landed")
        out_landed = sem("out_landed")
        consts_ready = sem("consts_ready")
        vec_ready = sem("vec_ready")
        xt_ready = sem("xt_ready")
        xt_read = sem("xt_read")
        sq_ready = sem("sq_ready")
        ss_ready = sem("ss_ready")
        root_ready = sem("root_ready")
        rstd_ready = sem("rstd_ready")
        xn_ready = sem("xn_ready")
        vt_ready = sem("vt_ready")
        th_ready = sem("th_ready")
        lam_ready = sem("lam_ready")
        ada_acc = sem("ada_acc")
        ada_sum = sem("ada_sum")
        ada_read = sem("ada_read")
        ada_step = sem("ada_step")
        hin_hi = sem("hin_hi")
        hin = sem("hin")
        hi_done = sem("hi_done")
        slab_done = sem("slab_done")
        slab_used = sem("slab_used")
        branch_out = sem("branch_out")
        bank_read = [sem(f"bank_read{b}") for b in range(GRING)]
        att_ready = sem("att_ready")
        att_read = sem("att_read")
        misc_ready = sem("misc_ready")
        misc_read = sem("misc_read")
        rel_ready = sem("rel_ready")
        bias_ready = sem("bias_ready")
        sel_ready = sem("sel_ready")
        dbias_ready = sem("dbias_ready")
        shift_ready = sem("shift_ready")
        prob_ready = sem("prob_ready")
        probT_ready = sem("probT_ready")
        y_ready = sem("y_ready")
        d_ready = sem("d_ready")
        yhi_ready = sem("yhi_ready")
        yb_ready = sem("yb_ready")
        gate_ready = sem("gate_ready")
        prod_ready = sem("prod_ready")
        added = sem("added")
        mhi_ready = sem("mhi_ready")
        m_ready = sem("m_ready")
        x2_ready = sem("x2_ready")
        f_hi_ready = sem("f_hi_ready")
        f_ready = sem("f_ready")
        f_sq = sem("f_sq")
        x3_ready = sem("x3_ready")
        nat_ready = sem("nat_ready")
        nat_sq = sem("nat_sq")
        o_ready = sem("o_ready")
        act_step = sem("act_step")
        dve_step = sem("dve_step")
        pool_step = sem("pool_step")
        pe_step = sem("pe_step")

        def slab_source(what):
            if what[0] == "ada":
                q = ADA[what[1]]
                return w_ada[0, :, q * SC:(q + 1) * SC].rearrange("(k p) n -> p k n", p=P)
            kind, name, n = W[what[1]]
            if kind == "proj":
                width = IDXW if name == "idx" else SC
                return w_in[0, :, COL[name]:COL[name] + width].rearrange("(k p) n -> p k n", p=P)
            if kind == "gate":
                return w_gate[0, "abcd".index(name), :, n * SC:(n + 1) * SC].rearrange("(k p) n -> p k n", p=P)
            if kind == "branch":
                return w_branch[0, "abcd".index(name)].rearrange("(k p) n -> p k n", p=P)
            return w_out[0, :, n * SC:(n + 1) * SC].rearrange("(k p) n -> p k n", p=P)

        def raw_view(s, k, n):
            return raw[:, s % RAW, 0:k * n].rearrange("p (k n) -> p k n", k=k)

        def split_view(t, j, k=KT):
            return t[:, j % SPL, :].rearrange("p (k n) -> p k n", k=k)

        def landed(eng, s, chunks=0):
            eng.wait_ge(raw_landed[s % RAW], chunks * (16 * FF_ALL // RAW) + 16 * (s // RAW + 1))

        def bank_empty(eng, g):
            kind, n = EMPTY[g]
            eng.wait_ge({"bank": bank_read[g % GRING], "prod": prod_ready, "x2": x2_ready}[kind], n)

        def S0(h):
            return slice(h * P, (h + 1) * P)

        def S1(h):
            return slice(NH * P + h * SEQ, NH * P + (h + 1) * SEQ)

        MISC = ["vec", "shift", "iwT", "iw", "pv_a", "yt_a", "pv_b0", "pool", "pv_b1", "yt_b", "pv_d", "yt_d"]
        ATT = [("idx", 1), ("s_a", 1), ("t_a", 2), ("s_b0", 1), ("t_b0", 2), ("s_b1", 1),
               ("t_b1", 2), ("s_d", 1), ("t_d", 2)]
        attn = [n for n, _ in ATT]
        SOFT = ["a", "b0", "b1", "d"]
        YS = ["a", "c", "b", "d"]

        def misc_n(name):
            return MISC.index(name)

        def att_reads_before(name):
            return sum(r for _, r in ATT[:attn.index(name)])

        block = ctx.enter_context(nc.Block())

        @block.sync
        def _(sp):
            def rows(name, src):
                n = src.shape[0]
                sp.dma_start(vec[VROW[name]:VROW[name] + n, :], src).then_inc(vec_landed, 16)
            rows("c", c[0].rearrange("(r n) -> r n", n=P))
            rows("b_ada", b_ada[0].rearrange("(r n) -> r n", n=P))
            rows("norm1", norm1_g[0].rearrange("(r n) -> r n", n=P))
            rows("norm2", norm2_g[0].rearrange("(r n) -> r n", n=P))
            rows("b_gate", b_gate[0].rearrange("i (r n) -> (i r) n", n=P))
            rows("pool", pool_scale[0].rearrange("(r n) -> r n", n=P))
            sp.dma_start(x_nat, x[0].rearrange("(t p) d -> p t d", p=P)).then_inc(x_landed, 16)
            for s, what in enumerate(ORDER):
                if what[0] == "ada" and what[1] < NP:
                    i = what[1]
                    src = w_ada[0, :, i * SC:(i + 1) * SC].rearrange("(k p) n -> p k n", p=P)
                    sp.dma_start(shift_w[i], src).then_inc(shift_landed[i], 16)
                if s >= RAW:
                    sp.wait_ge(slab_done, s - RAW + 1)
                src = slab_source(what)
                sp.dma_start(raw_view(s, src.shape[1], src.shape[2]), src).then_inc(raw_landed[s % RAW], 16)
            with sp.Fori(0, DFF // DM) as ch:
                for k in range(FF_ALL):
                    s = NORD + k
                    sp.wait_ge(slab_done, ch * FF_ALL + (s - RAW + 1))
                    if k < NP:
                        src = w_ff1[0, :, bass.ts(ch * NP + k, SC)]
                    elif k == NP:
                        src = w_ada[0, :, bass.ts(ch + ADA[FADA], SC)]
                    else:
                        src = w_ff2[0, bass.ts(ch, DM), (k - NP - 1) * SC:(k - NP) * SC]
                    sp.dma_start(raw_view(s, KT, SC), src.rearrange("(k p) n -> p k n", p=P))\
                      .then_inc(raw_landed[s % RAW], 16)
            for t in range(TT):
                sp.wait_ge(o_ready, 2 * (t + 1))
                sp.dma_start(out[0, t * P:(t + 1) * P, :], merged[:, t * DM:(t + 1) * DM]).then_inc(out_landed, 16)
            sp.wait_ge(out_landed, 16 * TT)

        @block.gpsimd
        def _(pool):
            step = Count(pool_step)

            def settle(ins):
                step.inc(ins)
                pool.wait_ge(pool_step, step.n)

            settle(nc.gpsimd.memset(ident[:, :], 0.0))
            nc.gpsimd.affine_select(out=ident[:, :], in_=ident[:, :], compare_op=ALU.not_equal, fill=1.0, base=0,
                                    pattern=[[-1, P]], channel_multiplier=1).then_inc(consts_ready, 1)
            nc.gpsimd.memset(eps[:, :], EPS)
            nc.gpsimd.memset(zeros[:, :], 0.0)
            nc.gpsimd.memset(ones[:, :], 1.0).then_inc(consts_ready, 1)
            for t, lo, n in ((0, 0, P), (1, P, SEQ)):
                settle(nc.gpsimd.iota(causal[:, lo:lo + n], [[1, n]], base=-t * P, channel_multiplier=-1,
                                      allow_small_or_imprecise_dtypes=True))
                last = nc.gpsimd.affine_select(out=causal[:, lo:lo + n], in_=causal[:, lo:lo + n],
                                               compare_op=ALU.is_ge, fill=NEG, base=t * P, pattern=[[-1, n]],
                                               channel_multiplier=1)
            last.then_inc(consts_ready, 1)
            settle(nc.gpsimd.iota(icnt[:, :, :], [[0, 2], [1, SEQ]], base=1, channel_multiplier=0,
                                  allow_small_or_imprecise_dtypes=True))
            for g, wd in enumerate(WINDOWS):
                r = slice(HD * (g % 2), HD * (g % 2) + HD)
                settle(nc.gpsimd.tensor_scalar(icnt[r, g // 2, :], icnt[r, g // 2, :], float(wd), None, ALU.min))
            nc.gpsimd.memset(wpool[:, :, :], 0.0).then_inc(consts_ready, 1)
            nc.gpsimd.memset(win[:, :, 0:PAD], 0.0).then_inc(consts_ready, 1)
            pool.wait_ge(rstd_ready, 1)
            nc.gpsimd.tensor_tensor(xn, xT[:, :, :], rstd[:, :].unsqueeze(1).broadcast_to([P, KT, SEQ]),
                                    ALU.mult).then_inc(xn_ready, 1)
            pool.wait_ge(row_ready, 1)
            nc.gpsimd.memset(uT[:, :, 0:PAD], 0.0).then_inc(consts_ready, 1)
            pool.wait_ge(sel_ready, 1)
            pool.wait_ge(bias_ready, 3)
            for lo, n, at in ((0, P, 0), (P, SEQ, NH * P)):
                b = bias[2][:, at:at + NH * n].rearrange("p (h n) -> p h n", h=NH)
                last = nc.gpsimd.tensor_tensor(b, b, score[:, lo:lo + n].unsqueeze(1).broadcast_to([P, NH, n]), ALU.add)
            last.then_inc(dbias_ready, 1)
            for i in range(NP, NP * len(MIXERS)):
                n = i % NP
                pool.wait_ge(prod_ready, i + 1)
                m = merged[:, n * 2 * SEQ:(n + 1) * 2 * SEQ]
                if i >= 2 * NP:
                    pool.wait_ge(added, i - 2 * NP + 1)
                nc.gpsimd.tensor_tensor(m, m, prod[:, i % 2, :], ALU.add).then_inc(added, 1)
            pool.wait_ge(rstd_ready, 2)
            for k in range(KT):
                nc.gpsimd.tensor_tensor(xn[:, k, :], xT[:, k, :], rstd[:, :], ALU.mult).then_inc(xn_ready, 1)

        @block.scalar
        def _(act):
            step = Count(act_step)

            def settle(ins):
                step.inc(ins)
                act.wait_ge(act_step, step.n)

            act.dma_start(lamw[:, :], diff_lambda[0].rearrange("a b -> (a b)").partition_broadcast(P))\
               .then_inc(small_landed, 16)
            act.dma_start(subg[:, :], diff_subln_g[0].partition_broadcast(P)).then_inc(small_landed, 16)
            act.wait_ge(consts_ready, 5)
            for g in range(4):
                r = slice(HD * (g % 2), HD * (g % 2) + HD)
                act.dma_start(wpool[r, g // 2, r], w_pool[0, g]).then_inc(small_landed, 16)

            act.wait_ge(vt_ready, 1)
            nc.scalar.activation(cact[:, 0, :], vT[:, 0:KT], ACT.Tanh, scale=0.5).then_inc(th_ready, 1)
            act.wait_ge(x_landed, 16)
            for b in range(NP):
                act.wait_ge(xt_ready, b + 1)
                src = bank[b][:, :] if b < 3 else attf[:, 512:1024]
                nc.scalar.copy(xT[:, 2 * b:2 * b + 2, :].rearrange("p t s -> p (t s)"), src).then_inc(xt_read, 1)
            act.wait_ge(xt_read, NP)
            nc.scalar.activation(sq, xT[:, :, :], ACT.Square).then_inc(sq_ready, 1)

            def build_bias(i, sc):
                act.wait_ge(consts_ready, 3)
                act.wait_ge(row_ready, 2)
                for h in range(NH):
                    f = slope(3 * h + i) / sc
                    nc.scalar.activation(bias[i][:, S0(h)], causal[:, 0:P], ACT.Copy, scale=f)
                    last = nc.scalar.activation(bias[i][:, S1(h)], causal[:, P:P + SEQ], ACT.Copy, scale=f)
                last.then_inc(bias_ready, 1)

            act.wait_ge(ss_ready, 1)
            nc.scalar.activation(root[:, 0:2], attf[:, 0:2], ACT.Sqrt, bias=eps[:, 0:1], scale=1.0 / DM)\
                .then_inc(root_ready, 1)
            def hi(j):
                s = POS[("w", j)]
                landed(act, s)
                if j >= SPL:
                    act.wait_ge(slab_used, j - SPL + 1)
                if j == JP["idx"]:
                    r = raw_view(s, KT, IDXW)
                    v = split_view(w_hi, j)
                    q = NH * DHD
                    nc.scalar.copy(v[:, :, 0:q], r[:, :, 0:q])
                    for g in range(4):
                        nc.scalar.copy(v[:, :, q + g * DHD:q + (g + 1) * DHD], r[:, :, q:q + DHD])
                    nc.scalar.copy(iw_hi[:, :, :], r[:, :, q + DHD:IDXW]).then_inc(hi_done, 1)
                else:
                    nc.scalar.copy(w_hi[:, j % SPL, :], raw[:, s % RAW, :]).then_inc(hi_done, 1)

            hi(0)
            for i in range(2):
                act.wait_ge(row_ready, i + 1)
                if i == 1:
                    act.wait_ge(row_read, 1)
                nc.scalar.copy(shift_rows[i], attf[0:1, 1024:1536] if i == 0 else misc[0:1, :]).then_inc(row_read, 1)
            act.wait_ge(misc_ready, 1)
            nc.scalar.copy(mod[:, 0:KT], misc[:, 0:KT]).then_inc(misc_read, 1)
            for k in range(KT):
                act.wait_ge(xn_ready, 1)
                act.wait_ge(misc_read, 2)
                act.wait_ge(ada_read, k // 2 + 1)
                nc.scalar.activation(h_hi[:, k, :], xn[:, k, :], ACT.Identity, bias=mod[:, k:k + 1],
                                     scale=aff[:, 0, k:k + 1]).then_inc(hin_hi, 1)

            def hi_ff(k, ch):
                j = NW + k
                landed(act, NORD + k + (1 if k >= NP else 0), ch)
                act.wait_ge(slab_used, ch * FF_SLABS + (j - SPL + 1))
                nc.scalar.copy(w_hi[:, j % SPL, :], raw[:, (NORD + k + (1 if k >= NP else 0)) % RAW, :])\
                    .then_inc(hi_done, 1)

            def keep(dst, j):
                act.wait_ge(slab_used, j + 1)
                b = G[j] % GRING
                nc.scalar.copy(dst, bank[b][:, :].rearrange("p (t s) -> p t s", t=2)).then_inc(bank_read[b], 1)

            def soft(name, scale):
                r = SOFT.index(name)
                act.wait_ge(shift_ready, r + 1)
                for h in range(NH):
                    nc.scalar.activation(prob[:, S0(h)], prob[:, S0(h)], ACT.Exp, bias=nmax[:, h:h + 1], scale=scale,
                                         accum_out=rsum[:, h:h + 1])
                    last = nc.scalar.activation(prob[:, S1(h)], prob[:, S1(h)], ACT.Exp, bias=nmax[:, NH + h:NH + h + 1],
                                                scale=scale, accum_out=rsum[:, NH + h:NH + h + 1])
                last.then_inc(prob_ready, 1)

            def keep_probT(name):
                act.wait_ge(att_ready, attn.index("t_" + name) + 1)
                nc.scalar.copy(probT[:, 0:1024], attf[:, 0:1024]).then_inc(att_read, 1)

            def y_hi_of(name, user):
                i = YS.index(name)
                act.wait_ge(misc_ready, misc_n(user))
                if i >= 2:
                    act.wait_ge(slab_used, J[("branch", MIXERS[i - 2], 0)] + 1)
                src = misc[:, :].rearrange("p (t s) -> p t s", t=2)
                if user == "pool":
                    for t in range(2):
                        last = nc.scalar.activation(y_hi[:, i % 2, t, :], src[:, t, :], ACT.Copy,
                                                    scale=vT[:, VROW["pool"] + t:VROW["pool"] + t + 1])
                    last.then_inc(yhi_ready, 1)
                else:
                    nc.scalar.copy(y_hi[:, i % 2, :, :], src).then_inc(yhi_ready, 1)

            def gate(j):
                _, m, n = W[j]
                i = MIXERS.index(m)
                act.wait_ge(slab_used, j + 1)
                if i >= 1:
                    act.wait_ge(prod_ready, NP * (i - 1) + n + 1)
                b = G[j] % GRING
                for t in range(2):
                    col = "abcd".index(m) * KT + 2 * n + t
                    last = nc.scalar.activation(tg[:, n, t * SEQ:(t + 1) * SEQ], bank[b][:, t * SEQ:(t + 1) * SEQ],
                                                ACT.Tanh, bias=hgate[:, col:col + 1], scale=0.5)
                last.then_inc(bank_read[b], 1)

            for j in range(1, LEAD):
                hi(j)
            places = {"dq": dqT, "dk": dkT, "aq": qk_a, "ak": qk_b, "av": v0, "bq": qk_a, "bk": qk_b, "bv": v1,
                      "dv": v0, "idx": idxT}
            for j in range(NW + 1):
                if j >= 1:
                    kind, name, n = W[j - 1]
                    if kind == "proj":
                        keep(uT[:, :, PAD:] if name == "pu" else places[name], j - 1)
                    elif kind == "gate":
                        gate(j - 1)
                if j + LEAD < NW and j != NW - NP:
                    hi(j + LEAD)
                if j == 1:
                    act.wait_ge(misc_ready, misc_n("iwT"))
                    nc.scalar.copy(iwT[:, :], misc[0:NH, 0:SEQ]).then_inc(misc_read, 1)
                if j == 2:
                    act.wait_ge(att_ready, attn.index("idx") + 1)
                    nc.scalar.activation(prob, attf, ACT.Relu, scale=DHD ** -0.5).then_inc(att_read, 1)
                if j == 3:
                    build_bias(0, HD ** -0.5)
                if j == 4:
                    build_bias(1, DHD ** -0.5)
                if j == 5:
                    build_bias(2, HD ** -0.5)
                if j == 6:
                    act.wait_ge(lam_ready, 1)
                    nc.scalar.activation(lams[:, 2:4], lams[:, 0:2], ACT.Exp).then_inc(th_ready, 1)
                    soft("a", HD ** -0.5)
                if j == 8:
                    keep_probT("a")
                if j == 9:
                    soft("b0", DHD ** -0.5)
                if j == 10:
                    y_hi_of("a", "yt_a")
                if j == 11:
                    keep_probT("b0")
                if j == 12:
                    soft("b1", DHD ** -0.5)
                if j == 13:
                    y_hi_of("c", "pool")
                if j == 14:
                    keep_probT("b1")
                if j == 15:
                    soft("d", HD ** -0.5)
                if j == 17:
                    keep_probT("d")
                if j == 19:
                    y_hi_of("b", "yt_b")
                if j == 23:
                    y_hi_of("d", "yt_d")
                if j == NW - NP:
                    nc.scalar.activation(root[:, 3:4], eps[:, 0:1], ACT.Sqrt)
                    for n in range(NP):
                        act.wait_ge(added, NP * (len(MIXERS) - 2) + n + 1)
                        nc.scalar.mul(g_hi[:, 2 * n:2 * n + 2, :],
                                      merged[:, n * 2 * SEQ:(n + 1) * 2 * SEQ].rearrange("p (t s) -> p t s", t=2),
                                      0.5).then_inc(mhi_ready, 1)
                if j > NW - NP:
                    n = j - 1 - (NW - NP)
                    act.wait_ge(x2_ready, n + 1)
                    nc.scalar.activation(sq[:, 2 * n:2 * n + 2, :], xT[:, 2 * n:2 * n + 2, :], ACT.Square)\
                        .then_inc(sq_ready, 1)
                if j == NW - NP and j + LEAD < NW:
                    hi(j + LEAD)
                elif j + LEAD >= NW and j + LEAD - NW < NP - 1:
                    hi_ff(j + LEAD - NW, 0)
            act.wait_ge(ss_ready, 2)
            nc.scalar.activation(root[:, 0:2], attf[:, 0:2], ACT.Sqrt, bias=eps[:, 0:1], scale=1.0 / DM)\
                .then_inc(root_ready, 1)
            for k in range(KT):
                act.wait_ge(xn_ready, 2 + k)
                nc.scalar.activation(h_hi[:, k, :], xn[:, k, :], ACT.Identity, bias=mod[:, 24 + k:25 + k],
                                     scale=aff[:, 1, k:k + 1]).then_inc(hin_hi, 1)
            hi_ff(NP - 1, 0)
            act.dma_start(gf, final_norm_g.partition_broadcast(P)).then_inc(gf_landed, 16)

            def chunk(ch, last_chunk):
                for k in range(NP):
                    b = k % 2
                    act.wait_ge(slab_used, ch * FF_SLABS + (NW + k + 1))
                    nc.scalar.activation(tg[:, k, :], bank[b][:, :], ACT.Relu).then_inc(bank_read[b], 1)
                    act.wait_ge(bank_read[b], ch * 2 + (USES[b] + k // 2 + 1))
                    nc.scalar.activation(f_hi[:, 2 * k:2 * k + 2, :],
                                         tg[:, k, :].rearrange("p (t s) -> p t s", t=2), ACT.Square).then_inc(f_hi_ready, 1)
                    hi_ff(NP + k, ch)
                if not last_chunk:
                    for k in range(NP):
                        hi_ff(k, ch + 1)

            with act.Fori(0, DFF // DM - 1) as ch:
                chunk(ch, False)
            chunk(DFF // DM - 1, True)
            for half in range(2):
                for t in range(TT):
                    act.wait_ge(nat_ready, 2 * half + t + 1)
                    nc.scalar.activation(scratch[:, (2 * half + t) * 512:(2 * half + t + 1) * 512], natb[2 * t + half], ACT.Square,
                                         accum_out=rsum[:, 2 * t + half:2 * t + half + 1]).then_inc(nat_sq, 1)
            act.wait_ge(rstd_ready, 3)
            nc.scalar.activation(rinv[:, 0:2], nmax[:, 0:2], ACT.Sqrt, bias=eps[:, 0:1], scale=1.0 / DM)\
                .then_inc(root_ready, 1)

        @block.vector
        def _(dve):
            step = Count(dve_step)

            def settle(ins):
                step.inc(ins)
                dve.wait_ge(dve_step, step.n)

            V = nc.vector
            dve.wait_ge(vec_ready, 1)
            V.tensor_copy(vT[:, :], misc[:, 0:NVEC]).then_inc(vt_ready, 1)
            dve.wait_ge(vt_ready, 1)
            V.tensor_scalar(hgate[:, :], vT[:, VROW["b_gate"]:VROW["b_gate"] + NH * KT], 0.5, None, ALU.mult)\
             .then_inc(misc_read, 1)
            dve.wait_ge(th_ready, 1)
            settle(V.scalar_tensor_tensor(cact[:, 1, :], cact[:, 0, :], 1.0, vT[:, 0:KT], ALU.add, ALU.mult))
            V.tensor_scalar(cact[:, 0, :], cact[:, 1, :], 0.5, None, ALU.mult).then_inc(cact_ready, 1)
            dve.wait_ge(cact_ready, 1)

            def spread(n):
                dve.wait_ge(root_ready, n)
                settle(V.reciprocal(root[:, 0:2], root[:, 0:2]))
                for t in range(TT):
                    last = V.tensor_scalar(yn[:, t * P:(t + 1) * P], ident[:, :], root[:, t:t + 1], None, ALU.mult)
                last.then_inc(diag_ready, 1)
                dve.wait_ge(wide_ready, n)
                V.tensor_copy(rstd[:, :], attf[:, 0:SEQ]).then_inc(rstd_ready, 1)

            def ada_chain(a, s, ch=0, par=None):
                par = a % 2 if par is None else par
                landed(dve, s, ch)
                if a >= 2:
                    dve.wait_ge(ada_sum, ch + (a - 1 if a < FADA else a))
                r = raw_view(s, KT, SC)
                for k in range(KT):
                    o = acc[:, par, k % 2, :]
                    if k < 2:
                        ins = V.tensor_scalar(o, r[:, k, :], cact[:, 0, k:k + 1], None, ALU.mult)
                    else:
                        dve.wait_ge(ada_step, ch * KT + (KT * a + k - 1))
                        ins = V.scalar_tensor_tensor(o, r[:, k, :], cact[:, 0, k:k + 1], o, ALU.mult, ALU.add)
                    ins.then_inc(ada_step, 1)
                dve.wait_ge(ada_step, ch * KT + KT * (a + 1))
                V.tensor_tensor(acc[:, par, 0, :], acc[:, par, 0, :], acc[:, par, 1, :], ALU.add)\
                 .then_inc(slab_done, 1)

            def ada_keep(a, ch=0):
                q = ADA[a]
                dve.wait_ge(ada_sum, ch + (a + 1))
                if q in (4, 5, 6, 7, 16, 17, 18, 19):
                    i = 0 if q < 8 else 1
                    k = 2 * (q % 4)
                    settle(V.tensor_tensor(mod[:, 2 * q:2 * q + 2], adab[:, 0:2], vT[:, 8 + 2 * q:10 + 2 * q], ALU.add))
                    g = VROW["norm1"] if i == 0 else VROW["norm2"]
                    V.scalar_tensor_tensor(aff[:, i, k:k + 2], mod[:, 2 * q:2 * q + 2], 1.0, vT[:, g + k:g + k + 2],
                                           ALU.add, ALU.mult).then_inc(ada_read, 1)
                elif a >= FADA:
                    V.tensor_tensor(mod[:, bass.ds(ch * 2 + 2 * q, 2)], adab[:, 0:2],
                                    vT[:, bass.ds(ch * 2 + (8 + 2 * q), 2)], ALU.add).then_inc(ada_read, 1)
                else:
                    V.tensor_tensor(mod[:, 2 * q:2 * q + 2], adab[:, 0:2], vT[:, 8 + 2 * q:10 + 2 * q],
                                    ALU.add).then_inc(ada_read, 1)

            def h_lo_of(k, i):
                t = yn[:, (k % 2) * SEQ:(k % 2 + 1) * SEQ]
                dve.wait_ge(xn_ready, 2 + k if i == 1 else 1)
                if i == 0:
                    dve.wait_ge(misc_read, 2)
                    dve.wait_ge(ada_read, k // 2 + 1)
                settle(V.tensor_scalar(t, xn[:, k, :], aff[:, i, k:k + 1], mod[:, 24 * i + k:24 * i + k + 1],
                                       ALU.mult, ALU.add))
                dve.wait_ge(hin_hi, KT * i + k + 1)
                V.tensor_tensor(h_lo[:, k, :], t, h_hi[:, k, :].bitcast(F32), ALU.subtract).then_inc(hin, 1)

            def lo(j):
                s = POS[("w", j)]
                dve.wait_ge(hi_done, j + 1)
                if j == JP["idx"]:
                    r = raw_view(s, KT, IDXW)
                    v, vh = split_view(w_lo, j), split_view(w_hi, j)
                    q = NH * DHD
                    V.tensor_tensor(v[:, :, 0:q], r[:, :, 0:q], vh[:, :, 0:q].bitcast(F32), ALU.subtract)
                    for g in range(4):
                        c0, c1 = q + g * DHD, q + (g + 1) * DHD
                        V.tensor_tensor(v[:, :, c0:c1], r[:, :, q:q + DHD], vh[:, :, c0:c1].bitcast(F32), ALU.subtract)
                    V.tensor_tensor(iw_lo[:, :, :], r[:, :, q + DHD:IDXW], iw_hi[:, :, :].bitcast(F32), ALU.subtract)\
                     .then_inc(slab_done, 1)
                else:
                    V.tensor_tensor(w_lo[:, j % SPL, :], raw[:, s % RAW, :], w_hi[:, j % SPL, :].bitcast(F32),
                                    ALU.subtract).then_inc(slab_done, 1)

            ada_chain(0, POS[("ada", 0)])
            ada_chain(1, POS[("ada", 1)])
            spread(1)
            lo(0)
            for a in range(2, ADA0):
                ada_keep(a - 2)
                ada_chain(a, POS[("ada", a)])
            ada_keep(ADA0 - 2)
            for k in range(KT):
                if k == 2:
                    ada_keep(ADA0 - 1)
                h_lo_of(k, 0)
            dve.wait_ge(small_landed, 16 * 6)
            for i in range(2):
                a1, b1 = (2 * i) * DHD, (2 * i + 1) * DHD
                settle(V.tensor_tensor(yn[:, i * DHD:(i + 1) * DHD], lamw[:, a1:a1 + DHD], lamw[:, b1:b1 + DHD],
                                       ALU.mult))
            V.reduce_sum(lams[:, 0:2], yn[:, 0:2 * DHD].rearrange("p (i n) -> p i n", i=2), AX).then_inc(lam_ready, 1)
            settle(V.tensor_scalar(subg[:, :], subg[:, :], 1.0 - LAMBDA_INIT, None, ALU.mult))

            def lo_ff(k, ch):
                j = NW + k
                s = NORD + k + (1 if k >= NP else 0)
                dve.wait_ge(hi_done, ch * FF_SLABS + (j + 1))
                V.tensor_tensor(w_lo[:, j % SPL, :], raw[:, s % RAW, :], w_hi[:, j % SPL, :].bitcast(F32),
                                ALU.subtract).then_inc(slab_done, 1)

            def shift(name, i, scale):
                dve.wait_ge(att_ready, attn.index("s_" + name) + 1)
                if name == "d":
                    dve.wait_ge(dbias_ready, 1)
                if name in ("a", "b0"):
                    dve.wait_ge(bias_ready, i + 1)
                for h in range(NH):
                    V.tensor_tensor_reduce(out=prob[:, S0(h)], in0=attf[:, S0(h)], in1=bias[i][:, S0(h)], scale=1.0,
                                           scalar=-3e38, op0=ALU.add, op1=ALU.max, accum_out=smax[:, h:h + 1])
                    last = V.tensor_tensor_reduce(out=prob[:, S1(h)], in0=attf[:, S1(h)], in1=bias[i][:, S1(h)], scale=1.0,
                                                  scalar=-3e38, op0=ALU.add, op1=ALU.max,
                                                  accum_out=smax[:, NH + h:NH + h + 1])
                n = att_reads_before("s_" + name) + 1
                last.then_inc(att_read, 1)
                dve.wait_ge(att_read, n)
                V.tensor_scalar(nmax[:, :], smax[:, :], -scale, None, ALU.mult).then_inc(shift_ready, 1)

            def invert(name):
                dve.wait_ge(prob_ready, SOFT.index(name) + 1)
                settle(V.reciprocal(rinv[:, :], rsum[:, :]))

            def keep_probT(name):
                dve.wait_ge(att_ready, attn.index("t_" + name) + 1)
                V.tensor_copy(probT[:, 1024:1536], attf[:, 1024:1536]).then_inc(att_read, 1)

            def wide(t):
                return t.unsqueeze(2).broadcast_to([P, 8, HD])

            def heads(t):
                return t.rearrange("p (g d) -> p g d", d=HD)

            def y_lo_of(name, user):
                i = YS.index(name)
                dve.wait_ge(yhi_ready, i + 1)
                for t in range(2):
                    src = misc[:, t * SEQ:(t + 1) * SEQ]
                    if user == "pool":
                        last = V.scalar_tensor_tensor(y_lo[:, i % 2, t, :], src, vT[:, VROW["pool"] + t:VROW["pool"] + t + 1],
                                                      y_hi[:, i % 2, t, :].bitcast(F32), ALU.mult, ALU.subtract)
                    else:
                        last = V.tensor_tensor(y_lo[:, i % 2, t, :], src, y_hi[:, i % 2, t, :].bitcast(F32), ALU.subtract)
                last.then_inc(misc_read, 1)

            def topk(rounds):
                for _ in range(rounds):
                    for t, r in ((0, slice(0, P)), (1, slice(P, P + SEQ))):
                        V.max(top8[:, t, :], score[:, r])
                    settle(V.memset(lams[:, 6:7], 0.0))
                    for t, r in ((0, slice(0, P)), (1, slice(P, P + SEQ))):
                        ins = V.match_replace(score[:, r], top8[:, t, :], score[:, r], TAKEN)
                    settle(ins)

            def pool_windows(t):
                u = uT[:, t, :]
                cur, nxt = u, win[:, 0, :]
                w = 1
                small, large = WINDOWS[2 * t], WINDOWS[2 * t + 1]
                bufs = 0
                while w < small:
                    nxt = win[:, bufs % 2, :]
                    settle(V.tensor_tensor(nxt[:, PAD:], cur[:, PAD:], cur[:, PAD - w:PAD + SEQ - w], ALU.add))
                    cur, w, bufs = nxt, 2 * w, bufs + 1
                nxt = win[:, bufs % 2, :]
                V.tensor_tensor(nxt[HD:P, PAD:], cur[HD:P, PAD:], cur[HD:P, PAD - w:PAD + SEQ - w], ALU.add)
                settle(V.tensor_copy(nxt[0:HD, PAD:], cur[0:HD, PAD:]))
                settle(V.tensor_tensor(nxt[:, PAD:], nxt[:, PAD:], icnt[:, t, :], ALU.mult))
                return V.tensor_tensor(u[:, PAD:], nxt[:, PAD:], u[:, PAD:], ALU.subtract)

            def gated(jb, n):
                i = MIXERS.index(W[jb][1])
                g = G[jb] + n
                if n < NP - 1:
                    dve.wait_ge(branch_out, (NP - 1) * i + n + 1)
                else:
                    dve.wait_ge(slab_used, jb + 1)
                bank_empty(dve, G[jb - NP + n])
                if i == 0:
                    dst = merged[:, n * 2 * SEQ:(n + 1) * 2 * SEQ]
                else:
                    dst = prod[:, n % 2, :]
                    if NP * i + n - 2 >= NP:
                        dve.wait_ge(added, NP * (i - 1) + n - 1)
                V.scalar_tensor_tensor(dst, tg[:, n, :], 1.0, bank[g % GRING][:, :], ALU.add, ALU.mult)\
                 .then_inc(prod_ready, 1)

            for j in range(1, LEAD):
                lo(j)
            for j in range(NW + 1):
                if j >= 1 and W[j - 1][0] == "branch":
                    gated(j - 1, NP - 1)
                if j >= 1 and W[j - 1][0] == "out":
                    n = W[j - 1][2]
                    b = G[j - 1] % GRING
                    dve.wait_ge(slab_used, j)
                    for t in range(2):
                        k = 2 * n + t
                        last = V.scalar_tensor_tensor(xT[:, k, :], bank[b][:, t * SEQ:(t + 1) * SEQ], mod[:, 16 + k:17 + k],
                                                      xT[:, k, :], ALU.mult, ALU.add)
                    last.then_inc(x2_ready, 1)
                if j - 2 in ADA_GROUP:
                    ada_keep(ADA_GROUP[j - 2])
                if j == 1:
                    dve.wait_ge(consts_ready, 4)
                    settle(V.tensor_scalar(score[:, :], causal[:, :], NEG / 2, NEG, ALU.is_lt, ALU.mult))
                if j == 2:
                    dve.wait_ge(misc_ready, misc_n("iw"))
                    V.tensor_scalar(iw[:, :, :], misc[:, 0:TT * NH].rearrange("p (t h) -> p t h", t=TT),
                                    NH ** -0.5, None, ALU.mult).then_inc(misc_read, 1)
                    dve.wait_ge(misc_read, misc_n("iw") + 1)
                    dve.wait_ge(att_read, 1)
                    for h in range(NH):
                        for t, r, s in ((0, slice(0, P), S0(h)), (1, slice(P, P + SEQ), S1(h))):
                            ins = V.scalar_tensor_tensor(score[:, r], prob[:, s], iw[:, t, h:h + 1], score[:, r],
                                                         ALU.mult, ALU.add)
                        settle(ins)
                if j == 3 or j == 4:
                    topk(3)
                if j == 5:
                    topk(TOPK // 8 - 6)
                    V.tensor_scalar(score[:, :], score[:, :], TAKEN / 2, NEG, ALU.is_gt, ALU.mult).then_inc(sel_ready, 1)
                if j == 6:
                    shift("a", 0, HD ** -0.5)
                if j == 7:
                    invert("a")
                    settle(V.reciprocal(icnt[:, :, :], icnt[:, :, :]))
                if j == 8:
                    keep_probT("a")
                if j == 9:
                    dve.wait_ge(misc_ready, misc_n("pv_a"))
                    V.tensor_tensor(heads(yn[:, :]), heads(misc[:, :]), wide(rinv[:, :]), ALU.mult).then_inc(misc_read, 1)
                    shift("b0", 1, DHD ** -0.5)
                if j == 10:
                    y_lo_of("a", "yt_a")
                    invert("b0")
                if j == 11:
                    keep_probT("b0")
                    bank_empty(dve, G[JP["pu"]])
                    dve.wait_ge(consts_ready, 6)
                    settle(pool_windows(0))
                    pool_windows(1).then_inc(d_ready, 1)
                if j == 12:
                    dve.wait_ge(misc_ready, misc_n("pv_b0"))
                    V.tensor_tensor(heads(prod[:, 0, :]), heads(misc[:, :]), wide(rinv[:, :]), ALU.mult)\
                     .then_inc(misc_read, 1)
                    shift("b1", 1, DHD ** -0.5)
                    dve.wait_ge(th_ready, 2)
                    settle(V.tensor_tensor(lams[:, 4:5], lams[:, 2:3], lams[:, 3:4], ALU.subtract))
                    settle(V.tensor_scalar(lams[:, 5:6], lams[:, 4:5], LAMBDA_INIT, None, ALU.add))
                if j == 13:
                    y_lo_of("c", "pool")
                    invert("b1")
                    settle(V.tensor_scalar(rs[:, 0, :], rinv[:, :], lams[:, 5:6], None, ALU.mult))
                if j == 14:
                    keep_probT("b1")
                if j == 15:
                    dve.wait_ge(misc_ready, misc_n("pv_b1"))
                    V.tensor_tensor(heads(yn[:, :]), heads(misc[:, :]), wide(rs[:, 0, :]), ALU.mult).then_inc(misc_read, 1)
                    shift("d", 2, HD ** -0.5)
                if j == 17:
                    invert("d")
                    keep_probT("d")
                if j == 19:
                    y_lo_of("b", "yt_b")
                if j == 20:
                    dve.wait_ge(misc_ready, misc_n("pv_d"))
                    V.tensor_tensor(heads(yn[:, :]), heads(misc[:, :]), wide(rinv[:, :]), ALU.mult).then_inc(misc_read, 1)
                if j == 23:
                    y_lo_of("d", "yt_d")
                if j == NW - NP:
                    for n in range(NP):
                        dve.wait_ge(mhi_ready, n + 1)
                        V.scalar_tensor_tensor(g_lo[:, 2 * n:2 * n + 2, :].rearrange("p t s -> p (t s)"),
                                               merged[:, n * 2 * SEQ:(n + 1) * 2 * SEQ], 0.5,
                                               g_hi[:, 2 * n:2 * n + 2, :].rearrange("p t s -> p (t s)").bitcast(F32),
                                               ALU.mult, ALU.subtract).then_inc(m_ready, 1)
                if j < NW and W[j][0] == "branch":
                    for n in range(NP - 1):
                        gated(j, n)
                if j + LEAD < NW:
                    lo(j + LEAD)
                elif j + LEAD >= NW and j + LEAD - NW < NP - 1:
                    lo_ff(j + LEAD - NW, 0)
                if j in ADA_GROUP:
                    a = ADA_GROUP[j]
                    ada_chain(a, POS[("ada", a)])
                if j == 15:
                    settle(V.tensor_tensor(yn[:, :], prod[:, 0, :], yn[:, :], ALU.subtract))
                    settle(V.tensor_tensor(prod[:, 0, :], yn[:, :], yn[:, :], ALU.mult))
                    settle(V.reduce_sum(rs[:, 1, :], heads(prod[:, 0, :]), AX))
                    settle(V.tensor_scalar(rs[:, 1, :], rs[:, 1, :], 1.0 / HD, EPS, ALU.mult, ALU.add))
                if j == 16:
                    settle(V.tensor_scalar(rs[:, 2, :].bitcast(I32), rs[:, 1, :].bitcast(I32), -0.5, float(0x5F3759DF),
                                           ALU.mult, ALU.add))
                    settle(V.tensor_scalar(rs[:, 1, :], rs[:, 1, :], -0.5, None, ALU.mult))
                    for _ in range(4):
                        settle(V.tensor_tensor(rs[:, 3, :], rs[:, 2, :], rs[:, 2, :], ALU.mult))
                        settle(V.tensor_tensor(rs[:, 3, :], rs[:, 3, :], rs[:, 1, :], ALU.mult))
                        settle(V.scalar_tensor_tensor(rs[:, 2, :], rs[:, 3, :], 1.5, rs[:, 2, :], ALU.add, ALU.mult))
                if j == 17:
                    settle(V.tensor_tensor(heads(yn[:, :]), heads(yn[:, :]), wide(rs[:, 2, :]), ALU.mult))
                    V.tensor_tensor(heads(yn[:, :]), heads(yn[:, :]), subg[:, :].unsqueeze(1).broadcast_to([P, 8, HD]),
                                    ALU.mult).then_inc(y_ready, 1)
            spread(2)
            for k in range(KT):
                h_lo_of(k, 1)
            lo_ff(NP - 1, 0)
            ada_chain(FADA, NORD + NP, 0, 0)

            def chunk(ch, last_chunk):
                for k in range(NP):
                    b = k % 2
                    dve.wait_ge(bank_read[b], ch * 2 + (USES[b] + k // 2 + 1))
                    V.tensor_tensor(prod[:, b, :], tg[:, k, :], tg[:, k, :], ALU.mult).then_inc(f_sq, 1)
                    dve.wait_ge(f_sq, ch * NP + (k + 1))
                    dve.wait_ge(f_hi_ready, ch * NP + (k + 1))
                    V.tensor_tensor(f_lo[:, 2 * k:2 * k + 2, :].rearrange("p t s -> p (t s)"), prod[:, b, :],
                                    f_hi[:, 2 * k:2 * k + 2, :].rearrange("p t s -> p (t s)").bitcast(F32), ALU.subtract)\
                     .then_inc(f_ready, 1)
                    lo_ff(NP + k, ch)
                if not last_chunk:
                    for k in range(NP):
                        lo_ff(k, ch + 1)
                        if k == 2:
                            ada_keep(FADA, ch)
                    ada_chain(FADA, NORD + NP, ch + 1, 0)
                else:
                    ada_keep(FADA, ch)

            with dve.Fori(0, DFF // DM - 1) as ch:
                chunk(ch, False)
            chunk(DFF // DM - 1, True)
            dve.wait_ge(ada_read, len(ADA))
            for n in range(NP):
                dve.wait_ge(slab_used, NW + FF_SLABS * (DFF // DM - 1) + NP + n + 1)
                for t in range(2):
                    k = 2 * n + t
                    last = V.scalar_tensor_tensor(xT[:, k, :], accb[n][:, t * SEQ:(t + 1) * SEQ], mod[:, 40 + k:41 + k],
                                                  xT[:, k, :], ALU.mult, ALU.add)
                last.then_inc(x3_ready, 1)
            dve.wait_ge(nat_sq, 4)
            V.tensor_tensor(nmax[:, 0:2], rsum[:, 0:4:2], rsum[:, 1:4:2], ALU.add).then_inc(rstd_ready, 1)
            dve.wait_ge(root_ready, 3)
            settle(V.reciprocal(smax[:, 0:2], rinv[:, 0:2]))
            dve.wait_ge(gf_landed, 16)
            for t in range(TT):
                for half in range(2):
                    V.scalar_tensor_tensor(merged[:, t * DM + half * 512:t * DM + (half + 1) * 512], natb[2 * t + half],
                                           smax[:, t:t + 1], gf[:, half * 512:(half + 1) * 512], ALU.mult, ALU.mult)\
                     .then_inc(o_ready, 1)

        @block.tensor
        def _(pe):
            T = nc.tensor
            rows_done = Count(pe_step)

            def use_misc(name):
                if misc_n(name) > 0:
                    pe.wait_ge(misc_read, misc_n(name))

            def use_att(name):
                if att_reads_before(name) > 0:
                    pe.wait_ge(att_read, att_reads_before(name))

            pe.wait_ge(consts_ready, 1)
            pe.wait_ge(vec_landed, 16 * 6)
            T.transpose(misc[:, 0:NVEC], vec[0:NVEC, :], ident[0:NVEC, 0:NVEC]).then_inc(vec_ready, 1)
            pe.wait_ge(x_landed, 16)
            for b in range(NP):
                dst = bank[b][:, :] if b < 3 else attf[:, 512:1024]
                for k in (2 * b, 2 * b + 1):
                    for t in range(TT):
                        o = (k % 2) * SEQ + t * P
                        last = T.transpose(dst[:, o:o + P], x_nat[:, t, k * P:(k + 1) * P], ident[:, :])
                last.then_inc(xt_ready, 1)

            def sum_squares(first):
                for k in range(KT):
                    pe.wait_ge(sq_ready, 1 if first else 2 + k // 2)
                    for t in range(TT):
                        last = T.matmul(attf[:, t:t + 1], sq[:, k, t * P:(t + 1) * P], ones[:, 0:1],
                                        start=(k == 0 and t == 0), stop=(k == KT - 1), skip_group_check=True)
                last.then_inc(ss_ready, 1)

            def spread(n):
                pe.wait_ge(diag_ready, n)
                for t in range(TT):
                    last = T.matmul(attf[:, t * P:(t + 1) * P], ones[:, :], yn[:, t * P:(t + 1) * P], start=True, stop=True)
                last.then_inc(wide_ready, 1)

            def ada_total(a, ch=0, par=None):
                par = a % 2 if par is None else par
                pe.wait_ge(ada_acc_sem(a)[0], ada_acc_sem(a, ch)[1])
                if a >= 1:
                    pe.wait_ge(ada_read, ch + a)
                for t in range(2):
                    last = T.matmul(adab[:, t:t + 1], acc[:, par, 0, t * P:(t + 1) * P], ones[:, 0:1],
                                    start=True, stop=True)
                last.then_inc(ada_sum, 1)

            def ada_acc_sem(a, ch=0):
                s = POS[("ada", a)] if a < FADA else NORD + NP
                return slab_done, ch * FF_ALL + (s + 1)

            pe.wait_ge(consts_ready, 2)
            pe.wait_ge(cact_ready, 1)
            for i in range(NP):
                pe.wait_ge(shift_landed[i], 16)
                if i == 2:
                    pe.wait_ge(misc_read, 1)
                o = attf[0:1, 1024:1536] if i < 2 else misc[0:1, :]
                for k in range(KT):
                    last = T.matmul(o[:, (i % 2) * SC:(i % 2 + 1) * SC], cact[:, 0, k:k + 1], shift_w[i][:, k, :],
                                    start=(k == 0), stop=(k == KT - 1))
                if i % 2 == 1:
                    last.then_inc(row_ready, 1)
                if i == 0:
                    sum_squares(True)
                if i == 1:
                    spread(1)
                    ada_total(0)
            ada_total(1)
            pe.wait_ge(row_read, 2)
            T.matmul(misc[:, 0:KT], ident[:, :], vT[:, 8:8 + KT], start=True, stop=False, skip_group_check=True)
            for k in range(KT):
                last = T.matmul(misc[:, k:k + 1], shift_rows[k // 4][:, (k % 4) * P:(k % 4 + 1) * P], ones[0:1, 0:1],
                                start=False, stop=(k == KT - 1), skip_group_check=True)
            last.then_inc(misc_ready, 1)
            for a in range(2, ADA0):
                ada_total(a)

            def passes(o, lhs, rhs, first, last):
                (lh, ll), (rh, rl) = lhs, rhs
                T.matmul(o, lh, rh, start=first, stop=False, skip_group_check=True)
                T.matmul(o, lh, rl, start=False, stop=False, skip_group_check=True)
                return T.matmul(o, ll, rh, start=False, stop=last, skip_group_check=True)

            def use_bank(g):
                if g >= GRING:
                    bank_empty(pe, g - GRING)
                return bank[g % GRING]

            def project_T(j, xs, wait_x=None):
                pe.wait_ge(slab_done, POS[("w", j)] + 1)
                o = use_bank(G[j])
                wh, wl = split_view(w_hi, j), split_view(w_lo, j)
                for k in range(KT):
                    if wait_x is not None:
                        wait_x(k)
                    for t in range(2):
                        cols = slice(t * P, (t + 1) * P)
                        last = passes(o[:, t * SEQ:(t + 1) * SEQ], (wh[:, k, cols], wl[:, k, cols]),
                                      (xs[0][:, k, :], xs[1][:, k, :]), k == 0 and t == 0, k == KT - 1)
                last.then_inc(slab_used, 1)

            def project(j):
                pe.wait_ge(slab_done, POS[("w", j)] + 1)
                o = use_bank(G[j])
                wh, wl = split_view(w_hi, j), split_view(w_lo, j)
                for t in range(TT):
                    for k in range(KT):
                        tok = slice(t * P, (t + 1) * P)
                        last = passes(o[:, t * SC:(t + 1) * SC], (h_hi[:, k, tok], h_lo[:, k, tok]),
                                      (wh[:, k, :], wl[:, k, :]), k == 0 and t == 0, k == KT - 1)
                last.then_inc(slab_used, 1)

            def scores(name, groups, q, k, rows):
                use_att(name)
                for i, group in enumerate(groups):
                    for h in group:
                        qt, kt, r = q(h), k(h), rows(h)
                        T.matmul(attf[:, S0(h)], qt[r, 0:P], kt[r, 0:P], start=True, stop=True)
                        last = T.matmul(attf[:, S1(h)], qt[r, P:SEQ], kt[r, :], start=True, stop=True)
                    if i + 1 < len(groups):
                        rows_done.inc(last)
                        pe.wait_ge(pe_step, rows_done.n)
                last.then_inc(att_ready, 1)

            def transpose_probs(name):
                use_att("t_" + name)
                pe.wait_ge(prob_ready, SOFT.index(name) + 1)
                for i, at, w0 in ((0, S0, 0), (1, S1, 0), (2, S1, P)):
                    for h in range(NH):
                        c0 = at(h).start + w0
                        last = T.transpose(att[:, i, h * P:(h + 1) * P], prob[:, c0:c0 + P], ident[:, :])
                last.then_inc(att_ready, 1)

            def weigh(name, v):
                use_misc("pv_" + name)
                pe.wait_ge(att_read, att_reads_before("t_" + name) + 2)
                pt = probT.rearrange("p (i h q) -> p i h q", i=3, h=NH)
                for t in range(TT):
                    for h in range(NH):
                        o = misc[:, t * SC + h * HD:t * SC + (h + 1) * HD]
                        hv = slice(h * HD, (h + 1) * HD)
                        if t == 0:
                            T.matmul(o, pt[:, 0, h, :], v[:, 0, hv], start=True, stop=True)
                        else:
                            T.matmul(o, pt[:, 1, h, :], v[:, 0, hv], start=True, stop=False)
                            last = T.matmul(o, pt[:, 2, h, :], v[:, 1, hv], start=False, stop=True)
                last.then_inc(misc_ready, 1)

            def transpose_y(user):
                use_misc(user)
                for f in range(2):
                    for t in range(TT):
                        last = T.transpose(misc[:, f * SEQ + t * P:f * SEQ + (t + 1) * P],
                                           yn[:, t * SC + f * P:t * SC + (f + 1) * P], ident[:, :])
                last.then_inc(misc_ready, 1)

            h = (h_hi, h_lo)
            merged_parts = (g_hi, g_lo)
            half_rows = lambda hd: slice(HD * (hd % 2), HD * (hd % 2) + HD)
            even_odd = ((0, 2), (1, 3))

            for j, (kind, name, n) in enumerate(W):
                if kind == "proj":
                    if name in ("av", "bv", "dv"):
                        project(j)
                    else:
                        project_T(j, h, (lambda k: pe.wait_ge(hin, k + 1)) if j == 0 else None)
                elif kind == "gate":
                    project_T(j, h)
                elif kind == "branch":
                    i = MIXERS.index(name)
                    pe.wait_ge(misc_read, misc_n({"a": "yt_a", "c": "pool", "b": "yt_b", "d": "yt_d"}[name]) + 1)
                    pe.wait_ge(slab_done, POS[("w", j)] + 1)
                    wh, wl = split_view(w_hi, j, 2), split_view(w_lo, j, 2)
                    for m in range(NP):
                        o = use_bank(G[j] + m)
                        for t in range(2):
                            cols = slice(m * SC + t * P, m * SC + (t + 1) * P)
                            for k in range(2):
                                last = passes(o[:, t * SEQ:(t + 1) * SEQ], (wh[:, k, cols], wl[:, k, cols]),
                                              (y_hi[:, i % 2, k, :], y_lo[:, i % 2, k, :]), k == 0 and t == 0, k == 1)
                        last.then_inc(slab_used if m == NP - 1 else branch_out, 1)
                else:
                    project_T(j, merged_parts, (lambda k: pe.wait_ge(m_ready, k // 2 + 1)) if n == 0 else None)

                if j == 0:
                    use_misc("iwT")
                    for k in range(KT):
                        last = passes(misc[0:NH, 0:SEQ], (iw_hi[:, k, :], iw_lo[:, k, :]),
                                      (h_hi[:, k, :], h_lo[:, k, :]), k == 0, k == KT - 1)
                    last.then_inc(misc_ready, 1)
                if j == 1:
                    use_misc("iw")
                    for t in range(TT):
                        last = T.transpose(misc[:, t * NH:(t + 1) * NH], iwT[:, t * P:(t + 1) * P], ident[0:NH, 0:NH])
                    last.then_inc(misc_ready, 1)
                    bank_empty(pe, G[0])
                    scores("idx", [(hd,) for hd in range(NH)], lambda hd: idxT[:, 0, :], lambda hd: idxT[:, 1, :],
                           lambda hd: slice(DHD * hd, DHD * (hd + 1)))
                if j == 5:
                    bank_empty(pe, G[JP["ak"]])
                    scores("s_a", even_odd, lambda hd: qk_a[:, hd // 2, :], lambda hd: qk_b[:, hd // 2, :], half_rows)
                if j == 7:
                    transpose_probs("a")
                if j == 8:
                    weigh("a", v0)
                    bank_empty(pe, G[JP["bk"]])
                    scores("s_b0", even_odd, lambda hd: qk_a[:, hd // 2, :], lambda hd: qk_b[:, hd // 2, :],
                           lambda hd: slice(HD * (hd % 2), HD * (hd % 2) + DHD))
                if j == 9:
                    pe.wait_ge(misc_read, misc_n("pv_a") + 1)
                    transpose_y("yt_a")
                if j == 10:
                    transpose_probs("b0")
                if j == 11:
                    weigh("b0", v1)
                    scores("s_b1", even_odd, lambda hd: qk_a[:, hd // 2, :], lambda hd: qk_b[:, hd // 2, :],
                           lambda hd: slice(HD * (hd % 2) + DHD, HD * (hd % 2) + 2 * DHD))
                if j == 12:
                    use_misc("pool")
                    pe.wait_ge(d_ready, 1)
                    pe.wait_ge(small_landed, 16 * 6)
                    for t in range(2):
                        last = T.matmul(misc[:, t * SEQ:(t + 1) * SEQ], wpool[:, t, :], uT[:, t, PAD:], start=True, stop=True)
                    last.then_inc(misc_ready, 1)
                if j == 13:
                    transpose_probs("b1")
                if j == 14:
                    weigh("b1", v1)
                    scores("s_d", even_odd, lambda hd: dqT[:, hd // 2, :], lambda hd: dkT[:, hd // 2, :], half_rows)
                if j == 16:
                    transpose_probs("d")
                if j == 18:
                    pe.wait_ge(y_ready, 1)
                    transpose_y("yt_b")
                if j == 19:
                    weigh("d", v0)
                if j == 22:
                    pe.wait_ge(misc_read, misc_n("pv_d") + 1)
                    transpose_y("yt_d")
                if j - 1 in ADA_GROUP:
                    ada_total(ADA_GROUP[j - 1])

            sum_squares(False)
            spread(2)
            for n in range(NP):
                if n == 0:
                    pe.wait_ge(rstd_ready, 2)
                T.matmul(accb[n], zeros[:, :], zeros[:, 0:1].broadcast_to([P, 2 * SEQ]), start=True, stop=True)

            def chunk(ch):
                for k in range(NP):
                    j, s = NW + k, NORD + k
                    pe.wait_ge(slab_done, ch * FF_ALL + (s + 1))
                    b = k % 2
                    pe.wait_ge(bank_read[b], ch * 2 + (USES[b] + k // 2))
                    wh, wl = split_view(w_hi, j), split_view(w_lo, j)
                    for kt in range(KT):
                        if k == 0:
                            pe.wait_ge(hin, KT + kt + 1)
                        for t in range(2):
                            cols = slice(t * P, (t + 1) * P)
                            last = passes(bank[b][:, t * SEQ:(t + 1) * SEQ], (wh[:, kt, cols], wl[:, kt, cols]),
                                          (h_hi[:, kt, :], h_lo[:, kt, :]), kt == 0 and t == 0, kt == KT - 1)
                    last.then_inc(slab_used, 1)
                for k in range(NP):
                    j, s = NW + NP + k, NORD + NP + 1 + k
                    pe.wait_ge(slab_done, ch * FF_ALL + (s + 1))
                    wh, wl = split_view(w_hi, j), split_view(w_lo, j)
                    for kt in range(KT):
                        if k == 0 and kt % 2 == 0:
                            pe.wait_ge(f_ready, ch * NP + (kt // 2 + 1))
                        for t in range(2):
                            cols = slice(t * P, (t + 1) * P)
                            last = passes(accb[k][:, t * SEQ:(t + 1) * SEQ], (wh[:, kt, cols], wl[:, kt, cols]),
                                          (f_hi[:, kt, :], f_lo[:, kt, :]), False, kt == KT - 1)
                    last.then_inc(slab_used, 1)
                    if k == 1:
                        ada_total(FADA, ch, 0)

            with pe.Fori(0, DFF // DM) as ch:
                chunk(ch)
            pe.wait_ge(ada_read, len(ADA))
            for n in range(NP):
                pe.wait_ge(x3_ready, n + 1)
                for t in range(TT):
                    for k in (2 * n, 2 * n + 1):
                        o = (k % 4) * P
                        last = T.transpose(natb[2 * t + n // 2][:, o:o + P], xT[:, k, t * P:(t + 1) * P], ident[:, :])
                    if n % 2 == 1:
                        last.then_inc(nat_ready, 1)


_INS = ["x", "c", "w_ada", "b_ada", "norm1_g", "w_in", "diff_lambda", "diff_subln_g", "w_pool", "pool_scale",
        "w_gate", "b_gate", "w_branch", "w_out", "norm2_g", "w_ff1", "w_ff2", "final_norm_g"]


def kernel(**inputs):
    import concourse.bacc as bacc
    from concourse.bass_utils import run_bass_kernel_spmd

    nc = bacc.Bacc("TRN2", target_bir_lowering=False, num_devices=1)
    arrays, args = {}, []
    for name in _INS:
        a = np.ascontiguousarray(inputs[name])
        arrays[f"in_{name}"] = a
        args.append(nc.dram_tensor(f"in_{name}", a.shape, mybir.dt.from_np(a.dtype), kind="ExternalInput").ap())
    args.append(nc.dram_tensor("out_x", (1, SEQ, DM), F32, kind="ExternalOutput").ap())
    build(nc, *args)
    result = run_bass_kernel_spmd(nc, [arrays], core_ids=[0])
    return result.results[0]["out_x"]
```
